# Optimizing a Trainium2 kernel written in Bass

```python
import math
import jax, jax.numpy as jnp
from jax import lax
import numpy as np

D_MODEL = 1024
BATCH = 1
SEQ = 512
DEPTH = 2

HEAD_DIM = 64
A_HEADS = 6
A_PATTERNS = ((128, 1), (512, 4), (2048, 16))
B_HEADS = 6
C_Q_HEADS = 6
C_KV_HEADS = 2
C_GROUP = C_Q_HEADS // C_KV_HEADS
C_WINDOW = 128
N_BRANCHES = 3
A_WIDTH = A_HEADS * HEAD_DIM
B_WIDTH = B_HEADS * HEAD_DIM
C_Q_WIDTH = C_Q_HEADS * HEAD_DIM
C_KV_WIDTH = C_KV_HEADS * HEAD_DIM
IN_SIZES = (A_WIDTH, A_WIDTH, A_WIDTH, B_WIDTH, B_WIDTH, B_WIDTH, B_HEADS,
            C_Q_WIDTH, C_KV_WIDTH, C_KV_WIDTH, N_BRANCHES * D_MODEL)
IN_COLS = sum(IN_SIZES)
BLOCK = 128
ROPE_THETA = 10000.0
RMS_EPS = 1e-6
NEG_INF = -1e30
PEER_HEADS = 8
PEER_DK = 256
PEER_DK_HALF = PEER_DK // 2
N_KEYS = 128
N_EXPERTS = N_KEYS * N_KEYS
PEER_TOPK = 16
PEER_CHUNK = 128

kernel_name = "hybrid_dilated_fox_swasink_peer"

def rms_norm(x, g):
    x32 = x.astype(jnp.float32)
    y = x32 * lax.rsqrt(jnp.mean(x32 * x32, axis=-1, keepdims=True) + RMS_EPS)
    return (y * g.astype(jnp.float32)).astype(x.dtype)

def rope_tables(positions):
    inv_freq = ROPE_THETA ** (-jnp.arange(0, HEAD_DIM, 2, dtype=jnp.float32) / HEAD_DIM)
    ang = positions.astype(jnp.float32)[..., None] * inv_freq
    return jnp.cos(ang), jnp.sin(ang)

def apply_rope(t, cos, sin):
    t32 = t.astype(jnp.float32)
    t1, t2 = jnp.split(t32, 2, axis=-1)
    c = cos[:, :, None, :]
    s = sin[:, :, None, :]
    return jnp.concatenate([t1 * c - t2 * s, t2 * c + t1 * s], axis=-1).astype(t.dtype)

def split_columns(t):
    parts, start = [], 0
    for size in IN_SIZES:
        parts.append(t[..., start:start + size])
        start += size
    return parts

def banded_attention(q, k, v, max_dist, sink=None):
    n, length, hk, g, dh = q.shape
    nb = -(-length // BLOCK)
    pad = nb * BLOCK - length
    q = jnp.pad(q, ((0, 0), (0, pad), (0, 0), (0, 0), (0, 0)))
    kv_pad = ((0, 0), (BLOCK, pad), (0, 0), (0, 0))

    def windows(t):
        tb = jnp.pad(t, kv_pad).reshape(n, nb + 1, BLOCK, hk, dh)
        return jnp.concatenate([tb[:, :-1], tb[:, 1:]], axis=2)

    kw, vw = windows(k), windows(v)
    qb = q.reshape(n, nb, BLOCK, hk, g, dh)
    logits = jnp.einsum('nbqhgd,nbkhd->nbhgqk', qb, kw,
                        preferred_element_type=jnp.float32) * (dh ** -0.5)
    dist = jnp.arange(BLOCK)[:, None] + BLOCK - jnp.arange(2 * BLOCK)[None, :]
    band = (dist >= 0) & (dist <= max_dist)
    key_pos = jnp.arange(nb)[:, None] * BLOCK - BLOCK + jnp.arange(2 * BLOCK)[None, :]
    valid = band[None, :, :] & (key_pos >= 0)[:, None, :]
    logits = jnp.where(valid[None, :, None, None], logits, NEG_INF)
    m = jnp.max(logits, axis=-1, keepdims=True)
    if sink is not None:
        s = sink.astype(jnp.float32)[None, None, :, :, None, None]
        m = jnp.maximum(m, s)
    p = jnp.exp(logits - m)
    denom = jnp.sum(p, axis=-1, keepdims=True)
    if sink is not None:
        denom = denom + jnp.exp(s - m)
    out = jnp.einsum('nbhgqk,nbkhd->nbqhgd', p.astype(v.dtype), vw,
                     preferred_element_type=jnp.float32)
    out = out / jnp.transpose(denom, (0, 1, 4, 2, 3, 5))
    out = out.reshape(n, nb * BLOCK, hk, g, dh)[:, :length].astype(q.dtype)
    lse = jnp.transpose((m + jnp.log(denom))[..., 0], (0, 1, 4, 2, 3))
    lse = lse.reshape(n, nb * BLOCK, hk, g)[:, :length]
    return out, lse

def dilated_mixture_attention(q, k, v):
    b, s, h, dh = q.shape
    outs, lses = [], []
    for window, dil in A_PATTERNS:
        length = s // dil

        def to_res(t):
            return t.reshape(b, length, dil, h, dh).transpose(0, 2, 1, 3, 4).reshape(b * dil, length, h, dh)

        o, lse = banded_attention(to_res(q)[:, :, :, None, :], to_res(k), to_res(v), window // dil)
        outs.append(o[:, :, :, 0].reshape(b, dil, length, h, dh).transpose(0, 2, 1, 3, 4).reshape(b, s, h, dh))
        lses.append(lse[..., 0].reshape(b, dil, length, h).transpose(0, 2, 1, 3).reshape(b, s, h))
    wts = jax.nn.softmax(jnp.stack(lses, axis=0), axis=0)
    out = jnp.einsum('pbsh,pbshd->bshd', wts, jnp.stack(outs, axis=0).astype(jnp.float32))
    return out.astype(q.dtype)

def forgetting_attention(q, k, v, f_logit, b_f):
    b, s, h, dh = q.shape
    nq = s // BLOCK
    log_f = jax.nn.log_sigmoid(f_logit.astype(jnp.float32) + b_f.astype(jnp.float32))
    cum = jnp.cumsum(log_f, axis=1)
    cum_t = cum.transpose(0, 2, 1)
    key_pos = jnp.arange(s)
    qb = q.reshape(b, nq, BLOCK, h, dh).transpose(1, 0, 2, 3, 4)
    cb = cum_t.reshape(b, h, nq, BLOCK).transpose(2, 0, 1, 3)

    def block(args):
        q_blk, c_blk, i = args
        logits = jnp.einsum('bqhd,bkhd->bhqk', q_blk, k,
                            preferred_element_type=jnp.float32) * (dh ** -0.5)
        decay = c_blk[..., None] - cum_t[:, :, None, :]
        q_pos = i * BLOCK + jnp.arange(BLOCK)
        causal = key_pos[None, :] <= q_pos[:, None]
        p = jax.nn.softmax(jnp.where(causal, logits + decay, NEG_INF), axis=-1)
        return jnp.einsum('bhqk,bkhd->bqhd', p.astype(v.dtype), v,
                          preferred_element_type=jnp.float32).astype(q.dtype)

    out = lax.map(block, (qb, cb, jnp.arange(nq)))
    return out.transpose(1, 0, 2, 3, 4).reshape(b, s, h, dh)

def hybrid_mixer(xn, cos, sin, w_in, b_forget, sinks, b_gate, w_br_a, w_br_b, w_br_c, w_out):
    b, s, _ = xn.shape
    proj = jnp.einsum('bsd,dc->bsc', xn, w_in)
    qa, ka, va, qb, kb, vb, fb, qc, kc, vc, gate_logits = split_columns(proj)

    def heads(t, n):
        return t.reshape(b, s, n, HEAD_DIM)

    oa = dilated_mixture_attention(apply_rope(heads(qa, A_HEADS), cos, sin),
                                   apply_rope(heads(ka, A_HEADS), cos, sin),
                                   heads(va, A_HEADS)).reshape(b, s, A_WIDTH)
    ob = forgetting_attention(heads(qb, B_HEADS), heads(kb, B_HEADS), heads(vb, B_HEADS),
                              fb, b_forget).reshape(b, s, B_WIDTH)
    qc_r = apply_rope(heads(qc, C_Q_HEADS), cos, sin).reshape(b, s, C_KV_HEADS, C_GROUP, HEAD_DIM)
    kc_r = apply_rope(heads(kc, C_KV_HEADS), cos, sin)
    oc, _ = banded_attention(qc_r, kc_r, heads(vc, C_KV_HEADS), C_WINDOW - 1,
                             sink=sinks.reshape(C_KV_HEADS, C_GROUP))
    oc = oc.reshape(b, s, C_Q_WIDTH)
    gates = jax.nn.sigmoid(gate_logits.reshape(b, s, N_BRANCHES, D_MODEL) + b_gate)
    merged = (gates[:, :, 0] * (oa @ w_br_a)
              + gates[:, :, 1] * (ob @ w_br_b)
              + gates[:, :, 2] * (oc @ w_br_c))
    return merged @ w_out

def peer_ffn(xn, w_q, k1, k2, u, v):
    b, s, d = xn.shape
    xt = xn.reshape(-1, PEER_CHUNK, d)
    k1f = k1.astype(jnp.float32)
    k2f = k2.astype(jnp.float32)

    def chunk(xc):
        q = (xc @ w_q).reshape(PEER_CHUNK, PEER_HEADS, 2, PEER_DK_HALF).astype(jnp.float32)
        s1 = jnp.einsum('thd,nd->thn', q[:, :, 0], k1f)
        s2 = jnp.einsum('thd,nd->thn', q[:, :, 1], k2f)
        v1, i1 = lax.top_k(s1, PEER_TOPK)
        v2, i2 = lax.top_k(s2, PEER_TOPK)
        cand = (v1[..., :, None] + v2[..., None, :]).reshape(PEER_CHUNK, PEER_HEADS, PEER_TOPK * PEER_TOPK)
        cand_id = (i1[..., :, None] * N_KEYS + i2[..., None, :]).reshape(PEER_CHUNK, PEER_HEADS, PEER_TOPK * PEER_TOPK)
        top_s, top_pos = lax.top_k(cand, PEER_TOPK)
        ids = jnp.take_along_axis(cand_id, top_pos, axis=-1)
        g = jax.nn.softmax(top_s, axis=-1)
        act = jnp.einsum('thkd,td->thk', u[ids], xc, preferred_element_type=jnp.float32)
        w = (g * jax.nn.gelu(act, approximate=False)).astype(v.dtype)
        return jnp.einsum('thk,thkd->td', w, v[ids], preferred_element_type=jnp.float32).astype(xn.dtype)

    return lax.map(chunk, xt).reshape(b, s, d)

def setup_inputs(seed: int = 0) -> dict:
    key = jax.random.key(seed)
    ks = jax.random.split(key, 18)
    f32 = jnp.float32

    def nrm(k, shape, scale):
        return jax.random.normal(k, shape, f32) * scale

    return {
        "x": nrm(ks[0], (BATCH, SEQ, D_MODEL), 1.0),
        "positions": jnp.broadcast_to(jnp.arange(SEQ, dtype=jnp.int32), (BATCH, SEQ)),
        "norm1_g": 1.0 + nrm(ks[1], (DEPTH, D_MODEL), 0.05),
        "w_in": nrm(ks[2], (DEPTH, D_MODEL, IN_COLS), D_MODEL ** -0.5),
        "b_forget": 2.0 + nrm(ks[3], (DEPTH, B_HEADS), 0.5),
        "sinks": nrm(ks[4], (DEPTH, C_Q_HEADS), 0.5),
        "b_gate": nrm(ks[5], (DEPTH, N_BRANCHES, D_MODEL), 0.1),
        "w_br_a": nrm(ks[6], (DEPTH, A_WIDTH, D_MODEL), A_WIDTH ** -0.5),
        "w_br_b": nrm(ks[7], (DEPTH, B_WIDTH, D_MODEL), B_WIDTH ** -0.5),
        "w_br_c": nrm(ks[8], (DEPTH, C_Q_WIDTH, D_MODEL), C_Q_WIDTH ** -0.5),
        "w_out": nrm(ks[9], (DEPTH, D_MODEL, D_MODEL), D_MODEL ** -0.5),
        "norm2_g": 1.0 + nrm(ks[10], (DEPTH, D_MODEL), 0.05),
        "peer_wq": nrm(ks[11], (DEPTH, D_MODEL, PEER_HEADS * PEER_DK), D_MODEL ** -0.5),
        "peer_k1": nrm(ks[12], (DEPTH, N_KEYS, PEER_DK_HALF), PEER_DK_HALF ** -0.5),
        "peer_k2": nrm(ks[13], (DEPTH, N_KEYS, PEER_DK_HALF), PEER_DK_HALF ** -0.5),
        "peer_u": nrm(ks[14], (DEPTH, N_EXPERTS, D_MODEL), D_MODEL ** -0.5),
        "peer_v": nrm(ks[15], (DEPTH, N_EXPERTS, D_MODEL), PEER_HEADS ** -0.5),
        "final_g": 1.0 + nrm(ks[16], (D_MODEL,), 0.05),
    }

def reference(x, positions, norm1_g, w_in, b_forget, sinks, b_gate, w_br_a, w_br_b, w_br_c,
              w_out, norm2_g, peer_wq, peer_k1, peer_k2, peer_u, peer_v, final_g):
    cos, sin = rope_tables(positions)
    h = x
    for l in range(DEPTH):
        h = h + hybrid_mixer(rms_norm(h, norm1_g[l]), cos, sin, w_in[l], b_forget[l], sinks[l],
                             b_gate[l], w_br_a[l], w_br_b[l], w_br_c[l], w_out[l])
        h = h + peer_ffn(rms_norm(h, norm2_g[l]), peer_wq[l], peer_k1[l], peer_k2[l],
                         peer_u[l], peer_v[l])
    return rms_norm(h, final_g)


_drawn_inputs = setup_inputs


def setup_inputs(seed=0):
    import zlib

    import numpy as np

    out = dict(_drawn_inputs(seed))
    spreads = {}
    factors = {'sinks': 5.131}
    for name, (base, spread) in spreads.items():
        noise = np.random.default_rng([zlib.crc32(name.encode()), seed]).standard_normal(out[name].shape)
        drawn = base * np.exp(spread * noise) if base else spread * noise
        out[name] = __import__('jax').numpy.asarray(drawn.astype(out[name].dtype))
    for name, factor in factors.items():
        out[name] = (out[name] * factor).astype(out[name].dtype)
    return out
```

```python
from contextlib import ExitStack

import numpy as np
import concourse.bass as bass
from concourse import mybir

ALU = mybir.AluOpType
ACT = mybir.ActivationFunctionType
F32 = mybir.dt.float32
F32R = mybir.dt.float32r
I32 = mybir.dt.int32
U32 = mybir.dt.uint32
AX = mybir.AxisListType

P = 128
T, D = 512, 1024
NT, NK = T // P, D // P
DH = 64
HEADS = 6
HP = HEADS // 2
TOPK = 16
PH = 8
RMS_EPS = 1e-6
SCALE = DH ** -0.5
MASKED = -1e30 / SCALE

CW = 2048
KV_CHUNKS, KV_COLS = 2, 4 * DH
PROJ_CHUNKS, PROJ_COLS = 4, 226
V_COL = {0: 6 * P, 1: 7 * P, 2: P + PROJ_CHUNKS * PROJ_COLS}
F_COL = 8 * P
PROJ_W = V_COL[2] + P
C_ATT, C_MRG, C_OUT, C_WQ, C_U, C_V = KV_CHUNKS + HP * PROJ_CHUNKS, NK * 3, 4, PH, 64, 64
P_MRG = C_ATT // 2
P_OUT = P_MRG + C_MRG // 2
P_WQ = P_OUT + C_OUT // 2
P_U = P_WQ + C_WQ // 2
P_V = P_U + C_U // 2
PAIRS = P_V + C_V // 2
BRANCHES = 3
TRANSPOSED = [(1, 0, "q"), (2, 0, "k"), (3, 2, "q"), (0, 2, "k"), (4, 1, "q"), (5, 1, "k")]
UNITS = [(br, hh, qi) for br in (0, 2, 1) for hh in range(2) for qi in range(NT)]
NU = len(UNITS)
NG = NU // NT
LB = (4, 5, 2, 3)
LS = len(LB)
HB, FB = (4, 5, 2, 3, 0, 1), 6
F_AT = 6
NORM_AFTER, TURN_AFTER = 1, 2
O_HI, O_LO = 8, 9
FIND_STEPS = 7
G_STEPS, G_PER_STEP, G_TOK = 32, 4, 4
J_G = NT * FIND_STEPS // 2
J_TAIL = J_G + G_STEPS // 2
HALF = 64
TOPK_LINKS, LOOK_LINKS = 11, 10
ZEROED = 7
TWO_PI = 2 * np.pi
ROUND = 1.5 * 2.0 ** 23
PI_PARTS = (6.28125, 0.00193500518798828125, TWO_PI - 6.28125 - 0.00193500518798828125)
PI_BELOW = float(np.nextafter(np.float32(np.pi), np.float32(0)))


def wait_alone(eng, sem, value, passed):
    eng.wait_ge(sem, value)
    eng.sem_inc(passed, 1)


class Chain:

    def __init__(self, eng, sem, before, per, passed=None):
        self.eng, self.sem, self.before, self.per, self.n = eng, sem, before, per, 0
        self.passed = passed

    def __call__(self, ins):
        self.n += 1
        ins.then_inc(self.sem, 1)
        if self.passed:
            wait_alone(self.eng, self.sem, self.before + self.n, self.passed)
        else:
            self.eng.wait_ge(self.sem, self.before + self.n)

    def end(self):
        assert self.n == self.per, (self.n, self.per)


def bc(ap, axis, n):
    ap = ap.unsqueeze(axis)
    shape = list(ap.shape)
    shape[axis] = n
    return ap.broadcast_to(shape)


def blocks(br, qi):
    return list(range(max(0, qi - 1) if br == 2 else 0, qi + 1))


def build(nc, a, out):
    DEPTH = a["bgate"].shape[1]
    act_d = nc.dram_tensor("act_d", (P, P, T), F32, kind="Internal").ap()
    gate_d = nc.dram_tensor("gate_d", (T // HALF, P, P * HALF), F32, kind="Internal").ap()

    with ExitStack() as ctx:
        def sb(name, shape, dt=F32, to=ctx):
            return to.enter_context(nc.sbuf_tensor(name, shape, dt))

        def sem(name):
            return ctx.enter_context(nc.semaphore(name))

        ps = [ctx.enter_context(nc.psum_tensor(f"bank{i}", [P, T], F32)) for i in range(8)]

        h = sb("h", [P, NT, D])
        xT_hi, xT_lo = sb("xT_hi", [P, NK, T], F32R), sb("xT_lo", [P, NK, T], F32R)
        raw = [sb(f"raw{s}", [P, CW]) for s in range(2)]
        hi = [sb(f"hi{s}", [P, CW], F32R) for s in range(2)]
        lo = [sb(f"lo{s}", [P, CW], F32R) for s in range(2)]
        ident, iota = sb("ident_sb", [P, P]), sb("iota_sb", [P, P])
        mask = {0: sb("mask_a", [P, T]), 1: sb("mask_b", [P, T]), 2: sb("mask_c", [P, 2 * P])}
        select = sb("select_sb", [P, 2, P])
        norm_g = sb("norm_g", [P, 2 * DEPTH, NK])
        final_g = raw[1][:, 0:D]
        bgate = sb("bgate_sb", [P, DEPTH, 3 * NK])
        bforget = sb("bforget_sb", [2, DEPTH * HP])
        sink = sb("sink_sb", [P, DEPTH * HEADS])
        keysT = sb("keysT", [P, DEPTH, 2, P])
        cos, sin = sb("cos", [P, NT, 32]), sb("sin", [P, NT, 32])
        pos_i, pos_f = sb("pos_i", [P, NT], I32), sb("pos_f", [P, NT])
        eps, one = sb("eps", [P, 1]), sb("one", [P, 1])
        zero_r = sb("zero_r", [P, T], F32R)
        ss, rms, rstd = sb("ss", [P, NT]), sb("rms", [P, NT]), sb("rstd", [P, NT])
        mx, nmx = sb("mx", [P, NU]), sb("nmx", [P, NU])
        den, esink, rden = sb("den", [P, NU]), sb("esink", [P, NU]), sb("rden", [P, NU])

        mixer = ExitStack()
        oT_hi = sb("oT_hi", [P, HP * BRANCHES, T], F32R, mixer)
        oT_lo = sb("oT_lo", [P, HP * BRANCHES, T], F32R, mixer)
        heads = ExitStack()
        proj = sb("proj", [P, NT, PROJ_W], to=heads)
        kv = sb("kv", [P, NT, 4, 2, DH], to=heads)
        qT = {br: [sb(f"qT{br}{hh}", [P, T], to=heads) for hh in range(2)] for br in range(3)}
        kT = {br: sb(f"kT{br}", [P, T], to=heads) for br in range(3)}
        cum = sb("cum", [P, T], to=heads)
        fg = sb("fg", [2, 2, T], to=heads)
        lg = sb("lg", [P, LS, T], to=heads)
        pT = sb("pT", [P, 2, T], to=heads)
        heads.close()
        merge = ExitStack()
        mg_hi, mg_lo = sb("mg_hi", [P, NK, T], F32R, merge), sb("mg_lo", [P, NK, T], F32R, merge)
        gates = sb("gates", [P, 2, T], to=merge)
        acc, part = sb("acc", [P, T], to=merge), sb("part", [P, T], to=merge)
        merge.close()
        normed = ExitStack()
        xs = sb("xs", [P, NT, D], to=normed)
        normed.close()
        mixer.close()
        idx1T, idx2T = sb("idx1T", [P, T]), sb("idx2T", [P, T])
        gT = sb("gT", [P, T])
        onehot = sb("onehot", [P, G_PER_STEP, G_TOK, 2, P])
        act_s = sb("act_s", [P, 2, 2, T])
        find = ExitStack()
        scores = sb("scores", [P, PH, 2, NT, P], to=find)
        qhT = sb("qhT", [P, 2, 2, T], to=find)
        top_s, top_p = sb("top_s", [P, P], to=find), sb("top_p", [P, P], U32, find)
        top_i = sb("top_i", [P, 2, P], U32, find)
        vals = sb("vals", [P, 2, TOPK], to=find)
        left, cand, cand2 = sb("left", [P, P], to=find), sb("cand", [P, 256], to=find), sb("cand2", [P, 256], to=find)
        look = sb("look", [P, P, TOPK], to=find)
        slot_of = sb("slot_of", [P, 2, P], U32, find)
        idx_t = sb("idx_t", [P, 2, P], to=find)
        g_t, g_sum = sb("g_t", [P, P], to=find), sb("g_sum", [P, PH], to=find)
        find.close()
        table = ExitStack()
        gate_s = sb("gate_s", [P, 2, P, HALF], to=table)
        table.close()
        weigh = ExitStack()
        act_in = sb("act_in", [P, 2, 2, T], to=weigh)
        gate_in = sb("gate_in", [P, 2, T // HALF, 2, HALF], to=weigh)
        w_hi, w_lo = sb("w_hi", [P, 2, 2, T], F32R, weigh), sb("w_lo", [P, 2, 2, T], F32R, weigh)
        weigh.close()

        consts_in = sem("consts_in")
        pe_passed, dve_passed, pool_passed = sem("pe_passed"), sem("dve_passed"), sem("pool_passed")
        raw_in = [sem(f"raw_in{s}") for s in range(2)]
        hi_done, lo_done, w_used = sem("hi_done"), sem("lo_done"), sem("w_used")
        tables_link, tables_ready, angle_ready = sem("tables_link"), sem("tables_ready"), sem("angle_ready")
        zeros_ready, rows_zeroed = sem("zeros_ready"), sem("rows_zeroed")
        h_done, square_link, rstd_link, xs_done, x_ps, x_hi, x_lo = (
            sem(n) for n in ("h_done", "square_link", "rstd_link", "xs_done", "x_ps", "x_hi", "x_lo"))
        kv_ev, kv_link, kv_copied = sem("kv_ev"), sem("kv_link"), sem("kv_copied")
        proj_ev, rope_link, heads_ps, heads_act, heads_dve = (
            sem(n) for n in ("proj_ev", "rope_link", "heads_ps", "heads_act", "heads_dve"))
        f_ps, f_x, f_act, f_link = sem("f_ps"), sem("f_x"), sem("f_act"), sem("f_link")
        s_ps, mx_link, lg_done, ex_done, den_link, pn_done, tr_done, pt_done, pv_done, o_hi, o_lo = (
            sem(n) for n in ("s_ps", "mx_link", "lg_done", "ex_done", "den_link", "pn_done", "tr_done",
                             "pt_done", "pv_done", "o_hi", "o_lo"))
        sig_done, gated, acc_link, mg_hi_done, mg_lo_done, out_added = (
            sem(n) for n in ("sig_done", "gated", "acc_link", "mg_hi_done", "mg_lo_done", "out_added"))
        q_ev, sc_ps, sc_ev = sem("q_ev"), sem("sc_ps"), sem("sc_ev")
        tile_link, topk_link, look_link, shift_ready, exp_ready, idx_ps, idx_ev = (
            sem(n) for n in ("tile_link", "topk_link", "look_link", "shift_ready", "exp_ready", "idx_ps", "idx_ev"))
        u0_ps, gelu0, gelu1, act_stored = sem("u0_ps"), sem("gelu0"), sem("gelu1"), sem("act_stored")
        act_out = [sem(f"act_out{s}") for s in range(2)]
        oh_done, g_ps, g_ev, gate_free = sem("oh_done"), sem("g_ps"), sem("g_ev"), sem("gate_free")
        gate_out = [sem(f"gate_out{s}") for s in range(2)]
        gate_ld = [sem(f"gate_ld{s}") for s in range(2)]
        act_ld = [sem(f"act_ld{s}") for s in range(2)]
        prod_done, w_hi_done, w_done, y_ps, y_link = (
            sem(n) for n in ("prod_done", "w_hi_done", "w_done", "y_ps", "y_link"))
        final_in, out_ready, stored = sem("final_in"), sem("out_ready"), sem("stored")
        CR = 2

        loads = [(h, a["x"]), (ident, a["ident"]), (iota, a["iota"]), (mask[0], a["mask_a"]),
                 (mask[1], a["mask_b"]), (mask[2], a["mask_c"]), (select, a["select"]),
                 (norm_g, a["norm_g"]), (bgate, a["bgate"]),
                 (bforget, a["bforget"]), (sink, a["sink"]), (keysT, a["keysT"]), (pos_i, a["pos"]),
                 (sin, a["inv_freq"])]
        CONSTS = 16 * len(loads)

        block = ctx.enter_context(nc.Block())

        @block.sync
        def _(sp):
            for dst, src in loads:
                sp.dma_start(dst[:], src).then_inc(consts_in, 16)
            with sp.Fori(0, DEPTH * PAIRS) as p:
                for s in range(2):
                    sp.wait_ge(lo_done, 2 * p + s + 1)
                    sp.dma_start(raw[s][:], a["stream"][2 * p + s]).then_inc(raw_in[s], 16)
            sp.wait_ge(lo_done, 2 * DEPTH * PAIRS + 1)
            sp.dma_start(raw[0][:], a["stream"][2 * DEPTH * PAIRS]).then_inc(raw_in[0], 16)
            sp.wait_ge(lo_done, 2 * DEPTH * PAIRS + CR)
            sp.dma_start(final_g, a["final_g"]).then_inc(final_in, 16)
            for tt in range(NT):
                sp.wait_ge(out_ready, tt + 1)
                sp.dma_start(out[tt], xs[:, tt]).then_inc(stored, 16)
            sp.wait_ge(stored, 16 * NT)

        @block.gpsimd
        def _(pool):
            pool.memset(zero_r[:].bitcast(F32), 0.0).then_inc(zeros_ready, 1)
            pool.sem_inc(act_stored, CR)
            pool.sem_inc(gate_free, CR)
            with pool.Fori(0, DEPTH) as l:
                lp = l * PAIRS
                wait_alone(pool, x_lo, NK * (2 * l) + NK, pool_passed)
                link = Chain(pool, rows_zeroed, ZEROED * l, ZEROED, passed=pool_passed)
                for br in range(3):
                    link(pool.memset(qT[br][0][DH:P, :], 0.0))
                    link(pool.memset(qT[br][1][0:DH, :], 0.0))
                link(pool.memset(cum[:], 0.0))
                link.end()
                wait_alone(pool, kv_link, 6 * (l + 1), pool_passed)
                with pool.Fori(0, HP) as hp:
                    b = l * HP + hp
                    wait_alone(pool, o_lo, NG * b + 1, pool_passed)
                    for x, col in enumerate((0, V_COL[2])):
                        pool.tensor_copy(proj[:, :, col:col + P],
                                         kv[:].rearrange("p t m c d -> p t (m c d)")[:, :, bass.ds(hp * DH + 2 * x * P, P)]
                                         ).then_inc(kv_copied, 1)

                def split_lo(p, s):
                    pool.wait_ge(hi_done, 2 * p + s + 1)
                    pool.tensor_tensor(lo[s][:], raw[s][:], hi[s][:].bitcast(F32), ALU.subtract).then_inc(lo_done, 1)

                def step(p, s, split=False):
                    wait_alone(pool, gelu1, 2 * p[0] + s + 2, pool_passed)
                    pool.dma_start(act_d[bass.ds(4 * p[1] + 2 * s, 2)].rearrange("i j t -> j i t"),
                                   act_s[:, s]).then_inc(act_out[s], 16)
                    if split:
                        split_lo(lp + P_U + p[1] + 1, s)
                    pool.wait_ge(act_out[s], 16 * p[0] + 16)
                    pool.sem_inc(act_stored, 1)

                wait_alone(pool, lo_done, 2 * (lp + P_U) + 1 + CR, pool_passed)
                split_lo(lp + P_U, 1)
                with pool.Fori(0, J_G - 1) as j:
                    for s in range(2):
                        step((l * (C_U // 2) + j, j), s, split=True)
                for s in range(2):
                    step((l * (C_U // 2) + J_G - 1, J_G - 1), s, split=s == 0)

                def half_tiles(w, first):
                    for sl in range(2):
                        for st in range(4):
                            j = w * 4 + sl * 2 + st // 2 + J_G
                            step((l * (C_U // 2) + j, j), st % 2)
                            if st == 1 and not (first and sl == 0):
                                pool.wait_ge(gate_out[1 - sl], 16 * (l * 4 + w + sl))
                                pool.sem_inc(gate_free, 1)
                        wait_alone(pool, g_ev, (l * 8 + w * 2 + sl) * 16 + 16 + G_PER_STEP, pool_passed)
                        pool.dma_start(gate_d[w * 2 + sl], gate_s[:, sl].rearrange("p i t -> p (i t)")).then_inc(gate_out[sl], 16)

                half_tiles(0, True)
                with pool.Fori(1, 4) as w:
                    half_tiles(w, False)

                def load_step(j, s):
                    wait_alone(pool, w_done, 2 * (l * (C_V // 2) + j) + s + 1, pool_passed)
                    pool.dma_start(act_in[:, s], act_d[bass.ds(4 * j + 2 * s, 2)].rearrange("i j t -> j i t")).then_inc(act_ld[s], 16)
                    pool.dma_start(gate_in[:, s].rearrange("p h i t -> p h (i t)"),
                                   gate_d[:, :, bass.ds((4 * j + 2 * s) * HALF, 2 * HALF)].rearrange("h j f -> j h f")).then_inc(gate_ld[s], 16)

                step((l * (C_U // 2) + J_TAIL, J_TAIL), 0)
                step((l * (C_U // 2) + J_TAIL, J_TAIL), 1)
                pool.wait_ge(gate_out[1], 16 * (l * 4 + 4))
                pool.sem_inc(gate_free, 1)
                load_step(0, 0)
                load_step(0, 1)
                step((l * (C_U // 2) + J_TAIL + 1, J_TAIL + 1), 0)
                step((l * (C_U // 2) + J_TAIL + 1, J_TAIL + 1), 1)
                with pool.Fori(1, C_V // 2) as j:
                    for s in range(2):
                        load_step(j, s)

        @block.scalar
        def _(act):
            def split_hi(p, s):
                act.wait_ge(raw_in[s], 16 * p + 16)
                act.wait_ge(w_used, 2 * p + s + 1)
                act.activation(hi[s][:], raw[s][:], ACT.Copy).then_inc(hi_done, 1)

            def ahead(p, s):
                split_hi(p + s, 1 - s)

            act.sem_inc(q_ev, CR)
            act.sem_inc(sc_ev, CR)
            act.sem_inc(gelu0, 1)
            act.sem_inc(idx_ev, 1)
            act.sem_inc(gelu1, 1)
            act.sem_inc(g_ev, G_PER_STEP)
            act.wait_ge(consts_in, CONSTS)
            act.wait_ge(angle_ready, 1)
            act.activation(sin[:], sin[:], ACT.Sin)
            act.activation(cos[:], cos[:], ACT.Sin).then_inc(tables_ready, 1)
            split_hi(0, 0)

            def squares(q):
                act.wait_ge(h_done, q + 1)
                link = Chain(act, square_link, 2 * q, 2)
                for tt in range(NT):
                    last = act.activation(xs[:, tt], h[:, tt], ACT.Square, accum_out=ss[:, tt:tt + 1])
                link(last)
                link(act.activation(rms[:], ss[:], ACT.Sqrt, scale=1.0 / D, bias=eps[:, 0:1]))
                link.end()

            def x_split_hi(q):
                for k in range(NK):
                    act.wait_ge(x_ps, NK * q + k + 1)
                    act.activation(xT_hi[:, k], ps[k][:], ACT.Copy, scale=norm_g[:, q, k:k + 1]).then_inc(x_hi, 1)

            with act.Fori(0, DEPTH) as l:
                lp = l * PAIRS
                squares(2 * l)
                x_split_hi(2 * l)

                for s in range(KV_CHUNKS):
                    ahead(lp, s)
                act.wait_ge(w_used, 2 * lp + KV_CHUNKS + CR)
                for tt in range(NT):
                    for copy in range(2):
                        last = act.activation(kv[:, tt, :, copy],
                                              ps[4 + tt][:, 0:KV_COLS].rearrange("p (m d) -> p m d", m=4), ACT.Copy)
                last.then_inc(kv_ev, 1)

                with act.Fori(0, HP) as hp:
                    b = l * HP + hp
                    for c in range(PROJ_CHUNKS):
                        p, s = lp + KV_CHUNKS // 2 + hp * (PROJ_CHUNKS // 2) + c // 2, c % 2
                        ahead(p, s)
                        act.wait_ge(w_used, 2 * p + s + 1 + CR)
                        for tp in range(2):
                            last = act.activation(
                                proj[:, 2 * tp:2 * tp + 2, P + c * PROJ_COLS:P + (c + 1) * PROJ_COLS],
                                ps[2 * s + tp][:].rearrange("p (a c) -> p a c", a=2)[:, :, 0:PROJ_COLS], ACT.Copy)
                        last.then_inc(proj_ev, 1)
                    act.wait_ge(rows_zeroed, ZEROED * (l + 1))
                    for x, (_, br, what) in enumerate(TRANSPOSED):
                        act.wait_ge(heads_ps, 6 * b + x + 1)
                        if what == "q":
                            act.activation(qT[br][0][0:DH, :], ps[HB[x]][0:DH, :], ACT.Copy).then_inc(heads_act, 1)
                        else:
                            act.activation(kT[br][:], ps[HB[x]][:], ACT.Copy).then_inc(heads_act, 1)
                    for u in range(NU + O_HI - NT + 1):
                        if u == F_AT:
                            link = Chain(act, f_act, 3 * b, 3)
                            act.wait_ge(f_x, b + 1)
                            link(act.activation(fg[:, 1], fg[:, 0], ACT.Abs))
                            link(act.activation(fg[:, 1], fg[:, 1], ACT.Exp, scale=-1.0))
                            link(act.activation(fg[:, 1], fg[:, 1], ACT.Ln, bias=one[0:2, 0:1]))
                            link.end()
                        if u < NU:
                            br, hh, qi = UNITS[u]
                            nk = len(blocks(br, qi)) * P
                            act.wait_ge(lg_done, NU * b + u + 1)
                            last = act.activation(lg[:, u % LS, 0:nk], lg[:, u % LS, 0:nk], ACT.Exp,
                                                  bias=nmx[:, u:u + 1], accum_out=den[:, u:u + 1])
                            if br == 2:
                                sk = sink[:, bass.ds(l * HEADS + hp * 2 + hh, 1)]
                                last = act.activation(esink[:, u:u + 1], sk, ACT.Exp, bias=nmx[:, u:u + 1])
                            last.then_inc(ex_done, 1)
                        v = u - TURN_AFTER
                        if 0 <= v < NU:
                            nk = len(blocks(UNITS[v][0], UNITS[v][2])) * P
                            act.wait_ge(tr_done, NU * b + v + 1)
                            if v >= 2:
                                act.wait_ge(pv_done, NU * b + v - 1)
                            act.activation(pT[:, v % 2, 0:nk], ps[6 + v % 2][:, 0:nk], ACT.Copy).then_inc(pt_done, 1)
                        if u >= O_HI and (u - O_HI) % NT == 0:
                            g = (u - O_HI) // NT
                            br, hh, _ = UNITS[4 * g]
                            rows = slice(hh * DH, hh * DH + DH)
                            act.wait_ge(pv_done, NU * b + 4 * g + 4)
                            act.activation(oT_hi[rows, bass.ds(hp * 3 + br, 1), :].rearrange("p o t -> p (o t)"),
                                           ps[g % 2][rows, :], ACT.Copy).then_inc(o_hi, 1)

                with act.Fori(0, NK // 2) as j:
                    for m in range(6):
                        p, s, M = lp + P_MRG + 3 * j + m // 2, m % 2, l * C_MRG + 6 * j + m
                        cb, br = 2 * j + m // 3, m % 3
                        ahead(p, s)
                        act.wait_ge(w_used, 2 * p + s + 1 + CR)
                        act.wait_ge(gated, M + 1)
                        act.activation(gates[:, s], ps[s][:], ACT.Sigmoid,
                                       bias=bgate[:, l, bass.ds(cb * 3 + br, 1)]).then_inc(sig_done, 1)
                        if br == 2:
                            act.wait_ge(acc_link, 2 * (l * NK + cb) + 2)
                            act.activation(mg_hi[:, cb], acc[:], ACT.Copy).then_inc(mg_hi_done, 1)

                with act.Fori(0, C_OUT // 2) as j:
                    for s in range(2):
                        ahead(lp + P_OUT + j, s)

                squares(2 * l + 1)
                x_split_hi(2 * l + 1)

                def q_evac(n, s):
                    act.wait_ge(w_used, 2 * (lp + P_WQ) + n + 1 + CR)
                    act.wait_ge(sc_ps, l * PH + n + 1)
                    for half in range(2):
                        last = act.activation(qhT[:, s, half], ps[2 * s + half][:], ACT.Copy)
                    last.then_inc(q_ev, 1)

                def s_evac(n, s):
                    act.wait_ge(sc_ps, l * PH + n + 1 + CR)
                    for half in range(2):
                        last = act.activation(scores[:, n, half], ps[4 + 2 * s + half][:].rearrange("p (a n) -> p a n", a=NT), ACT.Copy)
                    last.then_inc(sc_ev, 1)

                split_hi(lp + P_WQ, 1)
                q_evac(0, 0)

                def q_steps(j, last_pair):
                    for s in range(2):
                        if not (last_pair and s == 1):
                            split_hi(lp + P_WQ + j + 1, s)
                            q_evac(2 * j + s + 1, 1 - s)
                        s_evac(2 * j + s, s)

                with act.Fori(0, PH // 2 - 1) as j:
                    q_steps(j, False)
                q_steps(PH // 2 - 1, True)

                def gelu(j, s, which):
                    k = l * C_U + 2 * j + s
                    if which == 0:
                        act.wait_ge(u0_ps, k + 1)
                        act.wait_ge(act_stored, k + 1)
                        act.activation(act_s[:, s, 0], ps[0][:], ACT.Gelu).then_inc(gelu0, 1)
                    else:
                        act.wait_ge(w_used, 2 * (lp + P_U + j) + s + 1 + CR)
                        act.activation(act_s[:, s, 1], ps[1][:], ACT.Gelu).then_inc(gelu1, 1)

                with act.Fori(0, NT // 2) as th:
                    for st in range(2 * FIND_STEPS):
                        tt = th * 2 + st // FIND_STEPS
                        ahead(lp + P_U + th * FIND_STEPS + st // 2, st % 2)
                        if st % FIND_STEPS == FIND_STEPS - 1:
                            act.wait_ge(shift_ready, l * NT + tt + 1)
                            act.activation(g_t[:], g_t[:], ACT.Exp).then_inc(exp_ready, 1)
                        gelu(th * FIND_STEPS + st // 2, st % 2, 0)
                        gelu(th * FIND_STEPS + st // 2, st % 2, 1)
                        if st % FIND_STEPS == FIND_STEPS - 1:
                            act.wait_ge(idx_ps, l * NT + tt + 2)
                            tok = bass.ds(tt * P, P)
                            act.activation(idx1T[:, tok], ps[2][:, 0:P], ACT.Copy)
                            act.activation(idx2T[:, tok], ps[2][:, P:2 * P], ACT.Copy)
                            act.activation(gT[:, tok], ps[2][:, 2 * P:3 * P], ACT.Copy).then_inc(idx_ev, 1)

                def g_evac(w, sl, q):
                    ht = l * 8 + w * 2 + sl
                    act.wait_ge(g_ps, ht * 16 + q + 1 + G_PER_STEP)
                    if q == 0:
                        act.wait_ge(gate_free, ht + 1)
                    src = ps[4 + q % G_PER_STEP][:].rearrange("p (t i) -> p i t", t=G_TOK)
                    dst = gate_s[:, bass.ds(sl, 1), :, q * G_TOK:(q + 1) * G_TOK].rearrange("p o i t -> p (o i) t")
                    act.activation(dst, src, ACT.Copy).then_inc(g_ev, 1)

                with act.Fori(0, 4) as w:
                    with act.Fori(0, 2) as sl:
                        for st in range(4):
                            j, s = w * 4 + sl * 2 + st // 2 + J_G, st % 2
                            ahead(lp + P_U + j, s)
                            g_evac(w, sl, 4 * st)
                            gelu(j, s, 0)
                            g_evac(w, sl, 4 * st + 1)
                            g_evac(w, sl, 4 * st + 2)
                            gelu(j, s, 1)
                            g_evac(w, sl, 4 * st + 3)

                def weights_hi(k, s):
                    act.wait_ge(prod_done, l * C_V + k + 1)
                    act.wait_ge(w_used, 2 * (lp + P_V) + k + 1)
                    act.activation(w_hi[:, s], act_in[:, s], ACT.Copy).then_inc(w_hi_done, 1)

                for n in range(4):
                    j, s = J_TAIL + n // 2, n % 2
                    ahead(lp + P_U + j, s)
                    gelu(j, s, 0)
                    gelu(j, s, 1)
                weights_hi(0, 0)

                def v_steps(j, last_pair):
                    for s in range(2):
                        ahead(lp + P_V + j, s)
                        if not (last_pair and s == 1):
                            weights_hi(2 * j + s + 1, 1 - s)

                with act.Fori(0, C_V // 2 - 1) as j:
                    v_steps(j, False)
                v_steps(C_V // 2 - 1, True)

            squares(2 * DEPTH)

        @block.vector
        def _(dve):
            def split_lo(p, s):
                dve.wait_ge(hi_done, 2 * p + s + 1)
                dve.tensor_tensor(lo[s][:], raw[s][:], hi[s][:].bitcast(F32), ALU.subtract).then_inc(lo_done, 1)

            def ahead(p, s):
                split_lo(p + s, 1 - s)

            dve.sem_inc(lo_done, CR)
            dve.sem_inc(o_lo, 1)
            dve.sem_inc(gated, CR)
            dve.sem_inc(out_added, CR)
            dve.sem_inc(w_done, CR)
            link = Chain(dve, tables_link, 0, 12)
            dve.memset(eps[:], RMS_EPS)
            dve.wait_ge(zeros_ready, 1)
            link(dve.memset(one[:], 1.0))
            dve.wait_ge(consts_in, CONSTS)
            dve.sem_inc(h_done, 1)
            link(dve.tensor_copy(pos_f[:], pos_i[:]))
            link(dve.tensor_tensor(sin[:], bc(pos_f[:], 2, 32), sin[:], ALU.mult))
            turns = lg[:, 0, 0:P].rearrange("p (a b) -> p a b", a=NT)
            link(dve.tensor_scalar(turns, sin[:], 1.0 / TWO_PI, ROUND, ALU.mult, ALU.add))
            link(dve.tensor_scalar(turns, turns, ROUND, None, ALU.subtract))
            for c in PI_PARTS:
                link(dve.scalar_tensor_tensor(out=sin[:], in0=turns, scalar=-c, in1=sin[:], op0=ALU.mult, op1=ALU.add))
            link(dve.tensor_scalar(sin[:], sin[:], -PI_BELOW, PI_BELOW, ALU.max, ALU.min))
            link(dve.tensor_scalar(turns, sin[:], TWO_PI / 4, -TWO_PI, ALU.is_gt, ALU.mult))
            link(dve.scalar_tensor_tensor(out=cos[:], in0=sin[:], scalar=TWO_PI / 4, in1=turns, op0=ALU.add, op1=ALU.add))
            link(dve.tensor_scalar(cos[:], cos[:], -PI_BELOW, PI_BELOW, ALU.max, ALU.min))
            link.end()
            dve.sem_inc(angle_ready, 1)
            split_lo(0, 0)

            def row_scales(q):
                link = Chain(dve, rstd_link, q, 1)
                dve.wait_ge(square_link, 2 * q + 2)
                link(dve.reciprocal(rstd[:], rms[:]))
                link.end()

            def x_split_lo(q):
                row_scales(q)
                for tt in range(NT):
                    dve.tensor_scalar(xs[:, tt], h[:, tt], rstd[:, tt:tt + 1], None, ALU.mult).then_inc(xs_done, 1)
                for k in range(NK):
                    dve.wait_ge(x_hi, NK * q + k + 1)
                    dve.scalar_tensor_tensor(out=xT_lo[:, k], in0=ps[k][:], scalar=norm_g[:, q, k:k + 1],
                                             in1=xT_hi[:, k].bitcast(F32), op0=ALU.mult, op1=ALU.subtract).then_inc(x_lo, 1)

            def o_split_lo(b, hp, g):
                br, hh, _ = UNITS[4 * g]
                rows = slice(hh * DH, hh * DH + DH)
                o = bass.ds(hp * 3 + br, 1)
                dve.wait_ge(o_hi, NG * b + g + 1)
                dve.tensor_tensor(oT_lo[rows, o, :].rearrange("p o t -> p (o t)"), ps[g % 2][rows, :],
                                  oT_hi[rows, o, :].rearrange("p o t -> p (o t)").bitcast(F32),
                                  ALU.subtract).then_inc(o_lo, 1)

            with dve.Fori(0, DEPTH) as l:
                lp = l * PAIRS
                x_split_lo(2 * l)

                def rotate(link, rot, part):
                    n = rot.shape[2]
                    t1, t2 = rot[:, :, :, 0], rot[:, :, :, 1]
                    s_b, c_b = bc(sin[:], 2, n), bc(cos[:], 2, n)
                    flat = lambda buf: buf[:].rearrange("p a t -> p (a t)")[:, 0:NT * n * 32].rearrange(
                        "p (t r d) -> p t r d", t=NT, r=n)
                    t2s, t1s = flat(lg), flat(pT)
                    if part == 0:
                        link(dve.tensor_tensor(t2s, t2, s_b, ALU.mult))
                        link(dve.tensor_tensor(t1s, t1, s_b, ALU.mult))
                        link(dve.tensor_tensor(t1, t1, c_b, ALU.mult))
                    else:
                        link(dve.tensor_tensor(t2, t2, c_b, ALU.mult))
                        link(dve.tensor_tensor(t1, t1, t2s, ALU.subtract))
                        link(dve.tensor_tensor(t2, t2, t1s, ALU.add))

                for s in range(KV_CHUNKS):
                    ahead(lp, s)
                dve.wait_ge(kv_ev, l + 1)
                dve.wait_ge(tables_ready, 1)
                link = Chain(dve, kv_link, 6 * l, 6, passed=dve_passed)
                keys = kv[:, :, 0:2].rearrange("p t m c (x d) -> p t (m c) x d", x=2)
                rotate(link, keys, 0)
                rotate(link, keys, 1)
                link.end()

                with dve.Fori(0, HP) as hp:
                    b = l * HP + hp
                    link = Chain(dve, rope_link, 6 * b, 6)
                    rot = proj[:, :, P:4 * P].rearrange("p t (r c d) -> p t r c d", r=6, c=2)
                    for c in range(PROJ_CHUNKS):
                        ahead(lp + KV_CHUNKS // 2 + hp * (PROJ_CHUNKS // 2) + c // 2, c % 2)
                        if c == 2:
                            dve.wait_ge(proj_ev, PROJ_CHUNKS * b + 2)
                        if c >= 2:
                            rotate(link, rot, c - 2)
                    link.end()
                    dve.wait_ge(rows_zeroed, ZEROED * (l + 1))
                    for x in (0, 2, 4):
                        dve.wait_ge(heads_ps, 6 * b + x + 1)
                        dve.tensor_copy(qT[TRANSPOSED[x][1]][1][DH:P, :], ps[HB[x]][DH:P, :]).then_inc(heads_dve, 1)
                    dve.wait_ge(f_ps, b + 1)
                    dve.tensor_scalar(fg[:, 0], ps[FB][0:2, :], bforget[:, bass.ds(b, 1)], None, ALU.add).then_inc(f_x, 1)

                    mx_chain = Chain(dve, mx_link, NU * b, NU)
                    den_chain = Chain(dve, den_link, (NU + 8) * b, NU + 8)
                    for u in range(NU + O_LO - NT + 1):
                        if u == F_AT + 2:
                            link = Chain(dve, f_link, 2 * b, 2)
                            dve.wait_ge(f_act, 3 * b + 3)
                            link(dve.scalar_tensor_tensor(out=fg[:, 0], in0=fg[:, 0], scalar=0.0, in1=fg[:, 1],
                                                          op0=ALU.min, op1=ALU.subtract))
                            link(dve.tensor_tensor_scan(cum[0:2, :], fg[:, 0], zero_r[0:2, :].bitcast(F32), 0.0, ALU.add, ALU.add))
                            link.end()
                        if u < NU:
                            br, hh, qi = UNITS[u]
                            nk = len(blocks(br, qi)) * P
                            m = mask[br]
                            m = m[:, 2 * P - nk:] if br == 2 else m[:, T - nk:]
                            if u >= LS:
                                dve.wait_ge(tr_done, NU * b + u - LS + 1)
                            wait_alone(dve, s_ps, NU * b + u + 1, dve_passed)
                            mx_chain(dve.tensor_tensor_reduce(
                                lg[:, u % LS, 0:nk], ps[LB[u % LS]][:, 0:nk], m, SCALE, -3e38, ALU.add, ALU.max,
                                mx[:, u:u + 1]))
                            if br == 2:
                                sk = sink[:, bass.ds(l * HEADS + hp * 2 + hh, 1)]
                                dve.tensor_scalar(nmx[:, u:u + 1], mx[:, u:u + 1], sk, -1.0, ALU.max, ALU.mult).then_inc(lg_done, 1)
                            else:
                                dve.tensor_scalar(nmx[:, u:u + 1], mx[:, u:u + 1], -1.0, None, ALU.mult).then_inc(lg_done, 1)
                        v = u - NORM_AFTER
                        if 0 <= v < NU:
                            br, hh, qi = UNITS[v]
                            nk = len(blocks(br, qi)) * P
                            d = den[:, v:v + 1]
                            dve.wait_ge(ex_done, NU * b + v + 1)
                            if br == 2:
                                den_chain(dve.tensor_tensor(d, d, esink[:, v:v + 1], ALU.add))
                            den_chain(dve.reciprocal(rden[:, v:v + 1], d))
                            dve.tensor_scalar(lg[:, v % LS, 0:nk], lg[:, v % LS, 0:nk], rden[:, v:v + 1], None,
                                              ALU.mult).then_inc(pn_done, 1)
                        if u >= O_LO and (u - O_LO) % NT == 0:
                            o_split_lo(b, hp, (u - O_LO) // NT)
                    mx_chain.end()
                    den_chain.end()

                with dve.Fori(0, NK // 2) as j:
                    for m in range(6):
                        p, s, M = lp + P_MRG + 3 * j + m // 2, m % 2, l * C_MRG + 6 * j + m
                        cb, br = 2 * j + m // 3, m % 3
                        ahead(p, s)
                        dve.wait_ge(sig_done, M + 1)
                        dst = acc if br == 0 else part
                        dve.tensor_tensor(dst[:], gates[:, s], ps[2 + s][:], ALU.mult).then_inc(gated, 1)
                        dve.wait_ge(gated, M + 1 + CR)
                        if br > 0:
                            dve.tensor_tensor(acc[:], acc[:], part[:], ALU.add).then_inc(acc_link, 1)
                            dve.wait_ge(acc_link, 2 * (l * NK + cb) + br)
                        if br == 2:
                            dve.wait_ge(mg_hi_done, l * NK + cb + 1)
                            dve.tensor_tensor(mg_lo[:, cb], acc[:], mg_hi[:, cb].bitcast(F32), ALU.subtract).then_inc(mg_lo_done, 1)
                            dve.wait_ge(mg_lo_done, l * NK + cb + 1)

                with dve.Fori(0, C_OUT // 2) as j:
                    for s in range(2):
                        p = lp + P_OUT + j
                        ahead(p, s)
                        dve.wait_ge(w_used, 2 * p + s + 1 + CR)
                        for tp in range(2):
                            hv = h[:, 2 * tp:2 * tp + 2, bass.ds((2 * j + s) * 256, 256)]
                            last = dve.tensor_tensor(hv, hv, ps[4 + 2 * s + tp][:].rearrange("p (a c) -> p a c", a=2), ALU.add)
                        last.then_inc(out_added, 1)
                dve.wait_ge(out_added, C_OUT * (l + 1) + CR)
                dve.sem_inc(h_done, 1)

                x_split_lo(2 * l + 1)

                split_lo(lp + P_WQ, 1)
                with dve.Fori(0, PH // 2 - 1) as j:
                    for s in range(2):
                        split_lo(lp + P_WQ + j + 1, s)
                split_lo(lp + P_WQ + PH // 2, 0)

                def topk(tt, hd):
                    link = Chain(dve, topk_link, ((l * NT + tt) * PH + hd) * TOPK_LINKS, TOPK_LINKS, passed=dve_passed)

                    def best16(v_, i_, src, rest):
                        link(dve.max(v_[:, 0:8], src))
                        dve.max_index(i_[:, 0:8], v_[:, 0:8], src)
                        link(dve.match_replace(rest, v_[:, 0:8], src, -3e38))
                        link(dve.max(v_[:, 8:16], rest))
                        return dve.max_index(i_[:, 8:16], v_[:, 8:16], rest)

                    of_head = slice(hd * TOPK, (hd + 1) * TOPK)
                    for half in range(2):
                        best16(vals[:, half], top_i[:, half, of_head], tile_scores[:, hd, half], left[:])
                    link(dve.tensor_tensor(cand[:].rearrange("p (a b) -> p a b", a=TOPK), bc(vals[:, 0], 2, TOPK),
                                           bc(vals[:, 1], 1, TOPK), ALU.add))
                    link(best16(top_s[:, of_head], top_p[:, of_head], cand[:], cand2[:]))
                    link.end()

                def lookups(tt):
                    by_head = lambda ap: ap.rearrange("p (h k) -> p h k", h=PH)
                    s_, g_ = by_head(top_s[:]), by_head(g_t[:])
                    dve.wait_ge(idx_ps, l * NT + tt + 1)
                    dve.tensor_tensor(g_, s_, bc(s_[:, :, 0], 2, TOPK), ALU.subtract).then_inc(shift_ready, 1)
                    link = Chain(dve, look_link, (l * NT + tt) * LOOK_LINKS, LOOK_LINKS)
                    dve.tensor_scalar(slot_of[:, 0], top_p[:], 4, None, ALU.logical_shift_right)
                    link(dve.tensor_scalar(slot_of[:, 1], top_p[:], TOPK - 1, None, ALU.bitwise_and))
                    for half in range(2):
                        link(dve.tensor_tensor(look[:], bc(slot_of[:, half], 2, TOPK), bc(iota[:, 0:TOPK], 1, P), ALU.is_equal))
                        look4 = look[:].rearrange("p (h k) a -> p h k a", h=PH)
                        link(dve.tensor_tensor(look4, look4, bc(by_head(top_i[:, half]), 2, TOPK), ALU.mult))
                        link(dve.tensor_reduce(idx_t[:, half], look[:], AX.X, ALU.add))
                    dve.wait_ge(exp_ready, l * NT + tt + 1)
                    link(dve.tensor_reduce(g_sum[:], g_, AX.X, ALU.add))
                    link(dve.reciprocal(g_sum[:], g_sum[:]))
                    link(dve.tensor_tensor(g_, g_, bc(g_sum[:], 2, TOPK), ALU.mult))
                    link.end()

                wait_alone(dve, sc_ev, PH * (l + 1) + CR, dve_passed)
                tile_scores = look[:].rearrange("p (h b n) a -> p h b (n a)", h=PH, b=2)
                with dve.Fori(0, NT) as tt:
                    link = Chain(dve, tile_link, l * NT + tt, 1, passed=dve_passed)
                    link(dve.tensor_copy(tile_scores, scores[:, :, :, tt]))
                    link.end()
                    for hd in range(PH):
                        topk(tt, hd)
                    lookups(tt)

                dve.wait_ge(lo_done, 2 * (lp + P_U + J_G) + 1 + CR)
                wait_alone(dve, idx_ev, NT * (l + 1) + 1, dve_passed)
                with dve.Fori(0, G_STEPS // 2) as it:
                    for s in range(2):
                        for b in range(G_PER_STEP):
                            if b == 2:
                                ahead(lp + P_U + J_G + it, s)
                            q = it * 8 + s * 4 + b
                            dve.wait_ge(g_ps, l * P + q + 1)
                            for r in range(G_TOK):
                                t = bass.ds(q * G_TOK + r, 1)
                                o = onehot[:, b, r]
                                dve.tensor_scalar(o[:, 0], iota[:], idx1T[:, t], gT[:, t], ALU.is_equal, ALU.mult)
                                last = dve.tensor_scalar(o[:, 1], iota[:], idx2T[:, t], None, ALU.is_equal)
                            last.then_inc(oh_done, 1)
                for n in range(4):
                    ahead(lp + P_U + J_TAIL + n // 2, n % 2)

                def weigh_step(j, s):
                    k = l * C_V + 2 * j + s
                    dve.wait_ge(act_ld[s], 16 * (l * (C_V // 2) + j) + 16)
                    dve.wait_ge(gate_ld[s], 16 * (l * (C_V // 2) + j) + 16)
                    a_ = act_in[:, s].rearrange("p i (h t) -> p i h t", t=HALF)
                    for i in range(2):
                        last = dve.tensor_tensor(a_[:, i], a_[:, i], gate_in[:, s, :, i], ALU.mult)
                    last.then_inc(prod_done, 1)
                    dve.wait_ge(prod_done, k + 1)
                    dve.wait_ge(w_hi_done, k + 1)
                    dve.tensor_tensor(w_lo[:, s], act_in[:, s], w_hi[:, s].bitcast(F32), ALU.subtract).then_inc(w_done, 1)

                weigh_step(0, 0)

                def v_steps(j, last_pair):
                    for s in range(2):
                        ahead(lp + P_V + j, s)
                        if not (last_pair and s == 1):
                            weigh_step(j + s, 1 - s)

                with dve.Fori(0, C_V // 2 - 1) as j:
                    v_steps(j, False)
                v_steps(C_V // 2 - 1, True)

                dve.wait_ge(y_ps, l + 1)
                for tt in range(NT):
                    for nh in range(2):
                        hv = h[:, tt, nh * T:(nh + 1) * T]
                        last = dve.tensor_tensor(hv, hv, ps[2 * tt + nh][:], ALU.add)
                last.then_inc(y_link, 1)
                dve.wait_ge(y_link, l + 1)
                dve.sem_inc(h_done, 1)

            row_scales(2 * DEPTH)
            dve.wait_ge(final_in, 16)
            for tt in range(NT):
                dve.scalar_tensor_tensor(out=xs[:, tt], in0=h[:, tt], scalar=rstd[:, tt:tt + 1], in1=final_g,
                                         op0=ALU.mult, op1=ALU.mult).then_inc(out_ready, 1)

        @block.tensor
        def _(pe):
            pe.sem_inc(w_used, CR)
            pe.sem_inc(sc_ps, CR)
            pe.sem_inc(idx_ps, 1)
            pe.sem_inc(g_ps, G_PER_STEP)
            pe.wait_ge(consts_in, CONSTS)
            pe.wait_ge(zeros_ready, 1)

            def take(p, s):
                pe.wait_ge(lo_done, 2 * p + s + 1 + CR)

            def product(dst, a_, b_, first, last):
                pe.matmul(dst, a_[0], b_[0], start=first, stop=False)
                pe.matmul(dst, a_[0], b_[1], start=False, stop=False)
                return pe.matmul(dst, a_[1], b_[0], start=False, stop=last)

            def chunk(s, width, k):
                return [x[:, 0:k * width].rearrange("p (k c) -> p k c", k=k) for x in (hi[s], lo[s])]

            def at(pair, *ix):
                return [x[(slice(None), *ix)] for x in pair]

            xT = (xT_hi, xT_lo)

            def tile(tt):
                return slice(tt * P, tt * P + P)

            def x_transposes(q):
                for tt in range(NT):
                    pe.wait_ge(xs_done, NT * q + tt + 1)
                    for k in range(NK):
                        last = pe.transpose(ps[k][:, tile(tt)], xs[:, tt, tile(k)], ident[:])
                        if tt == NT - 1:
                            last.then_inc(x_ps, 1)
                wait_alone(pe, x_lo, NK * q + NK, pe_passed)

            with pe.Fori(0, DEPTH) as l:
                lp = l * PAIRS
                x_transposes(2 * l)

                for s in range(KV_CHUNKS):
                    take(lp, s)
                    w = chunk(s, KV_COLS, NK // 2)
                    for tt in range(NT):
                        for k in range(NK // 2):
                            last = product(ps[4 + tt][:, 0:KV_COLS], at(xT, s * NK // 2 + k, tile(tt)), at(w, k),
                                           s == 0 and k == 0, s == 1 and k == NK // 2 - 1)
                    last.then_inc(w_used, 1)

                with pe.Fori(0, HP) as hp:
                    b = l * HP + hp
                    pe.wait_ge(o_lo, NG * b + 1)
                    for c in range(PROJ_CHUNKS):
                        s = c % 2
                        take(lp + KV_CHUNKS // 2 + hp * (PROJ_CHUNKS // 2) + c // 2, s)
                        if c >= 2:
                            pe.wait_ge(proj_ev, PROJ_CHUNKS * b + c - 1)
                        w = chunk(s, PROJ_COLS, NK)
                        for tt in range(NT):
                            dst = ps[2 * s + tt // 2][:, (tt % 2) * 256:(tt % 2) * 256 + PROJ_COLS]
                            for k in range(NK):
                                last = product(dst, at(xT, k, tile(tt)), at(w, k), k == 0, k == NK - 1)
                        last.then_inc(w_used, 1)
                    pe.wait_ge(proj_ev, PROJ_CHUNKS * (b + 1))
                    pe.wait_ge(kv_ev, l + 1)
                    pe.wait_ge(rope_link, 6 * b + 6)
                    for x, (role, _, _) in enumerate(TRANSPOSED):
                        if role == 0:
                            pe.wait_ge(kv_copied, 2 * b + 2)
                        for tt in range(NT):
                            last = pe.transpose(ps[HB[x]][:, tile(tt)], proj[:, tt, tile(role)], ident[:])
                        last.then_inc(heads_ps, 1)
                    for tt in range(NT):
                        last = pe.transpose(ps[FB][0:2, tile(tt)], proj[:, tt, F_COL:F_COL + 2], ident[:])
                    last.then_inc(f_ps, 1)

                    def logits(u):
                        br, hh, qi = UNITS[u]
                        bl = blocks(br, qi)
                        keys = slice(bl[0] * P, (qi + 1) * P)
                        dst = ps[LB[u % LS]][:, 0:len(bl) * P]
                        if u == 0:
                            pe.wait_ge(heads_act, 6 * b + 2)
                            pe.wait_ge(heads_dve, 3 * b + 1)
                        if u == 2:
                            pe.wait_ge(heads_act, 6 * b + 6)
                            pe.wait_ge(heads_dve, 3 * b + 3)
                            pe.wait_ge(f_x, b + 1)
                        if u >= LS:
                            pe.wait_ge(lg_done, NU * b + u - LS + 1)
                        if UNITS[u - 1][0] != br == 1:
                            pe.wait_ge(f_link, 2 * b + 2)
                        last = pe.matmul(dst, qT[br][hh][:, tile(qi)], kT[br][:, keys], start=True, stop=br != 1)
                        if br == 1:
                            last = pe.matmul(dst, select[:, hh], cum[:, keys], start=False, stop=True)
                        last.then_inc(s_ps, 1)

                    def turn(u):
                        br, _, qi = UNITS[u]
                        pe.wait_ge(pn_done, NU * b + u + 1)
                        if u >= 2:
                            pe.wait_ge(pt_done, NU * b + u - 1)
                        for n in range(len(blocks(br, qi))):
                            last = pe.transpose(ps[6 + u % 2][:, tile(n)], lg[:, u % LS, tile(n)], ident[:])
                        last.then_inc(tr_done, 1)

                    def values(u):
                        br, _, qi = UNITS[u]
                        g, bl = u // NT, blocks(br, qi)
                        pe.wait_ge(pt_done, NU * b + u + 1)
                        if qi == 0 and g >= 2:
                            pe.wait_ge(o_lo, NG * b + g)
                        for n, kb in enumerate(bl):
                            last = pe.matmul(ps[g % 2][:, tile(qi)], proj[:, kb, V_COL[br]:V_COL[br] + P],
                                             pT[:, u % 2, tile(n)], start=n == 0, stop=n == len(bl) - 1)
                        last.then_inc(pv_done, 1)

                    for u in range(LS - 1):
                        logits(u)
                    for u in range(NU):
                        if u + LS - 1 < NU:
                            logits(u + LS - 1)
                        turn(u)
                        if u >= 1:
                            values(u - 1)
                    values(NU - 1)

                wait_alone(pe, o_lo, NG * HP * (l + 1) + 1, pe_passed)
                with pe.Fori(0, NK // 2) as j:
                    for m in range(6):
                        s, br = m % 2, m % 3
                        take(lp + P_MRG + 3 * j + m // 2, s)
                        pe.wait_ge(gated, l * C_MRG + 6 * j + m + 1)
                        w = chunk(s, P, NK + HP)
                        for k in range(NK):
                            product(ps[s][:], at(w, k), at(xT, k), k == 0, k == NK - 1)
                        for k in range(HP):
                            last = product(ps[2 + s][:], at(w, NK + k), at((oT_hi, oT_lo), k * 3 + br), k == 0, k == HP - 1)
                        last.then_inc(w_used, 1)

                wait_alone(pe, mg_lo_done, NK * (l + 1), pe_passed)
                with pe.Fori(0, C_OUT // 2) as j:
                    for s in range(2):
                        take(lp + P_OUT + j, s)
                        pe.wait_ge(out_added, l * C_OUT + 2 * j + s + 1)
                        w = chunk(s, 256, NK)
                        for tt in range(NT):
                            dst = ps[4 + 2 * s + tt // 2][:, (tt % 2) * 256:(tt % 2) * 256 + 256]
                            for k in range(NK):
                                last = product(dst, at((mg_hi, mg_lo), k, tile(tt)), at(w, k), k == 0, k == NK - 1)
                        last.then_inc(w_used, 1)

                x_transposes(2 * l + 1)

                def queries(j, s):
                    take(lp + P_WQ + j, s)
                    pe.wait_ge(q_ev, l * PH + 2 * j + s + 1)
                    w = chunk(s, 256, NK)
                    for half in range(2):
                        for k in range(NK):
                            last = product(ps[2 * s + half][:], at(w, k, tile(half)), at(xT, k), k == 0, k == NK - 1)
                    last.then_inc(w_used, 1)

                def key_scores(j, s):
                    n = l * PH + 2 * j + s
                    pe.wait_ge(q_ev, n + 1 + CR)
                    pe.wait_ge(sc_ev, n + 1)
                    for half in range(2):
                        for tt in range(NT):
                            last = pe.matmul(ps[4 + 2 * s + half][:, tile(tt)], qhT[:, s, half, tile(tt)],
                                             keysT[:, bass.ds(l, 1), half].rearrange("p o n -> p (o n)"),
                                             start=True, stop=True)
                    last.then_inc(sc_ps, 1)

                def q_steps(j, last_pair):
                    for s in range(2):
                        if not (last_pair and s == 1):
                            queries(j + s, 1 - s)
                        key_scores(j, s)

                queries(0, 0)
                with pe.Fori(0, PH // 2 - 1) as j:
                    q_steps(j, False)
                q_steps(PH // 2 - 1, True)

                def experts(j, s, i, first=0, end=NK):
                    k = l * C_U + 2 * j + s
                    if first == 0:
                        if i == 0:
                            take(lp + P_U + j, s)
                        pe.wait_ge((gelu0, gelu1)[i], k + 1)
                    w = chunk(s, P, 2 * NK)
                    for kk in range(first, end):
                        last = product(ps[i][:], at(w, i * NK + kk), at(xT, kk), kk == 0, kk == NK - 1)
                    if end == NK:
                        last.then_inc(w_used if i else u0_ps, 1)

                with pe.Fori(0, NT // 2) as th:
                    for st in range(2 * FIND_STEPS):
                        for i in range(2):
                            experts(th * FIND_STEPS + st // 2, st % 2, i)
                        if st % FIND_STEPS == FIND_STEPS - 1:
                            tt = th * 2 + st // FIND_STEPS
                            pe.wait_ge(look_link, (l * NT + tt + 1) * LOOK_LINKS)
                            pe.wait_ge(idx_ev, l * NT + tt + 1)
                            pe.transpose(ps[2][:, 0:P], idx_t[:, 0], ident[:])
                            pe.transpose(ps[2][:, P:2 * P], idx_t[:, 1], ident[:])
                            pe.transpose(ps[2][:, 2 * P:3 * P], g_t[:], ident[:]).then_inc(idx_ps, 1)

                def gates_of(q, slot):
                    pe.wait_ge(oh_done, q + 1)
                    pe.wait_ge(g_ev, q + 1)
                    for r in range(G_TOK):
                        o = onehot[:, slot, r]
                        last = pe.matmul(ps[4 + slot][:, tile(r)], o[:, 1], o[:, 0], start=True, stop=True)
                    last.then_inc(g_ps, 1)

                with pe.Fori(0, G_STEPS // 2) as it:
                    for s in range(2):
                        for i in range(2):
                            for n in range(2):
                                experts(J_G + it, s, i, n * NK // 2, (n + 1) * NK // 2)
                                gates_of(l * P + it * 8 + s * 4 + 2 * i + n, 2 * i + n)
                for n in range(4):
                    for i in range(2):
                        experts(J_TAIL + n // 2, n % 2, i)

                pe.wait_ge(gelu0, C_U * (l + 1) + 1)
                pe.wait_ge(gelu1, C_U * (l + 1) + 1)
                pe.wait_ge(g_ev, P * (l + 1) + G_PER_STEP)
                for bank in range(8):
                    pe.matmul(ps[bank][:], zero_r[:, 0:P], zero_r[:], start=True, stop=False)
                with pe.Fori(0, C_V // 2) as j:
                    for s in range(2):
                        take(lp + P_V + j, s)
                        pe.wait_ge(w_done, l * C_V + 2 * j + s + 1 + CR)
                        v = chunk(s, T, 4)
                        for i in range(2):
                            for tt in range(NT):
                                ys = ps[2 * tt], ps[2 * tt + 1]
                                for wp, vp in ((w_hi, 0), (w_hi, 1), (w_lo, 0)):
                                    for nh in range(2):
                                        last = pe.matmul(ys[nh][:], wp[:, s, i, tile(tt)], v[vp][:, 2 * i + nh],
                                                         start=False, stop=False)
                        last.then_inc(w_used, 1)
                for bank in range(8):
                    last = pe.matmul(ps[bank][:], zero_r[:, 0:P], zero_r[:], start=False, stop=True)
                last.then_inc(y_ps, 1)


def constants():
    t, s = np.arange(P)[:, None], np.arange(T)[None, :]
    dist = t + (T - P) - s
    count = ((dist >= 0) & (dist <= P)).astype(np.float64)
    for dil in (4, 16):
        count += (dist >= 0) & (dist % dil == 0)
    mask_a = np.where(count > 0, np.log(np.maximum(count, 1)) / SCALE, MASKED)
    mask_b = np.where(dist >= 0, 0.0, MASKED)
    d2 = t + P - np.arange(2 * P)[None, :]
    mask_c = np.where((d2 >= 0) & (d2 < P), 0.0, MASKED)
    select = np.zeros((P, 2, P))
    for hh in range(2):
        select[hh, hh] = -1.0 / SCALE
    freq = np.float32(10000.0) ** (-np.arange(0, DH, 2, dtype=np.float32) / np.float32(DH))
    f = {"mask_a": mask_a, "mask_b": mask_b, "mask_c": mask_c, "select": select, "ident": np.eye(P),
         "iota": np.broadcast_to(np.arange(P), (P, P)), "inv_freq": np.broadcast_to(freq, (P, NT, DH // 2))}
    return {k: np.ascontiguousarray(v, dtype=np.float32) for k, v in f.items()}


def layout(x, positions, norm1_g, w_in, b_forget, sinks, b_gate, w_br_a, w_br_b, w_br_c, w_out, norm2_g,
           peer_wq, peer_k1, peer_k2, peer_u, peer_v, final_g):
    depth = w_in.shape[0]
    A = HEADS * DH
    at, n = {}, 0
    for name, size in (("qa", A), ("ka", A), ("va", A), ("qb", A), ("kb", A), ("vb", A), ("f", HEADS),
                       ("qc", A), ("kc", 2 * DH), ("vc", 2 * DH), ("gate", 3 * D)):
        at[name] = n
        n += size
    stream = np.zeros((depth * 2 * PAIRS + 1, P, CW), np.float32)
    head = np.arange(DH)
    for l in range(depth):
        n = l * 2 * PAIRS
        w = w_in[l].reshape(NK, P, -1)
        both = np.concatenate([w[:, :, at[name]:at[name] + 2 * DH] for name in ("kc", "vc")], axis=2)
        both = both.reshape(KV_CHUNKS, NK // 2, P, KV_COLS).transpose(0, 2, 1, 3)
        stream[n:n + KV_CHUNKS, :, :NK // 2 * KV_COLS] = both.reshape(KV_CHUNKS, P, -1)
        n += KV_CHUNKS
        for hp in range(HP):
            two = [2 * hp, 2 * hp + 1]
            cols = []
            for name in ("qa", "ka", "qc", "qb", "kb", "va", "vb"):
                for hd in two:
                    cols.append(at[name] + hd * DH + head)
            cols.append(at["f"] + np.array(two))
            cols = np.concatenate(cols)
            part = np.zeros((NK, P, PROJ_CHUNKS * PROJ_COLS), np.float32)
            part[:, :, :len(cols)] = w[:, :, cols]
            part = part.reshape(NK, P, PROJ_CHUNKS, PROJ_COLS).transpose(2, 1, 0, 3)
            stream[n:n + PROJ_CHUNKS, :, :NK * PROJ_COLS] = part.reshape(PROJ_CHUNKS, P, -1)
            n += PROJ_CHUNKS
        gate = w[:, :, at["gate"]:].reshape(NK, P, 3, NK, P).transpose(3, 2, 1, 0, 4)
        br = np.stack([w_br_a[l], w_br_b[l], w_br_c[l]]).reshape(3, HP, P, NK, P).transpose(3, 0, 2, 1, 4)
        both = np.concatenate([gate, br], axis=3)
        stream[n:n + C_MRG, :, :(NK + HP) * P] = both.reshape(C_MRG, P, -1)
        n += C_MRG
        stream[n:n + C_OUT] = w_out[l].reshape(NK, P, C_OUT, 256).transpose(2, 1, 0, 3).reshape(C_OUT, P, CW)
        n += C_OUT
        stream[n:n + C_WQ] = peer_wq[l].reshape(NK, P, PH, 256).transpose(2, 1, 0, 3).reshape(C_WQ, P, CW)
        n += C_WQ
        stream[n:n + C_U] = peer_u[l].reshape(C_U, 2, P, NK, P).transpose(0, 4, 1, 3, 2).reshape(C_U, P, CW)
        n += C_U
        stream[n:n + C_V] = peer_v[l].reshape(C_V, 2, P, D).transpose(0, 2, 1, 3).reshape(C_V, P, CW)
    norms = np.stack([norm1_g, norm2_g], axis=1).reshape(2 * depth, NK, P)
    out = {
        "stream": stream,
        "x": x.reshape(NT, P, D).transpose(1, 0, 2),
        "pos": positions.reshape(NT, P).T,
        "norm_g": norms.transpose(2, 0, 1),
        "final_g": np.broadcast_to(final_g, (P, D)),
        "bgate": b_gate.reshape(depth, 3, NK, P).transpose(3, 0, 2, 1).reshape(P, depth, 3 * NK),
        "bforget": b_forget.reshape(depth * HP, 2).T,
        "sink": np.broadcast_to(sinks.reshape(-1), (P, depth * HEADS)),
        "keysT": np.stack([peer_k1, peer_k2], axis=1).transpose(3, 0, 1, 2),
    }
    return {k: np.ascontiguousarray(v) for k, v in out.items()}


def kernel(**inputs):
    import concourse.bacc as bacc
    from concourse.bass_utils import run_bass_kernel_spmd

    arrays = {**layout(**{k: np.asarray(v) for k, v in inputs.items()}), **constants()}
    nc = bacc.Bacc("TRN2", target_bir_lowering=False, num_devices=1)
    aps = {k: nc.dram_tensor(f"in_{k}", v.shape, mybir.dt.from_np(v.dtype), kind="ExternalInput").ap()
           for k, v in arrays.items()}
    out = nc.dram_tensor("out", (NT, P, D), F32, kind="ExternalOutput").ap()
    build(nc, aps, out)
    r = run_bass_kernel_spmd(nc, [{f"in_{k}": v for k, v in arrays.items()}], core_ids=[0])
    return r.results[0]["out"].reshape(1, T, D)
```
